# Optimizing a Trainium2 kernel written in Bass

```python
import math
import jax, jax.numpy as jnp
from jax import lax
import numpy as np

D_MODEL = 2048
BATCH = 1
SEQ = 256
DEPTH = 2

N_MIXERS = 2
N_ATTN_LAYERS = (DEPTH + 1) // 2
N_SSM_LAYERS = DEPTH // 2

N_HEADS = 16
HEAD_DIM = D_MODEL // N_HEADS
DILATED_GROUPS = ((128, 1), (512, 4), (2048, 16))
N_DGROUPS = len(DILATED_GROUPS)
ATTN_BLOCK = 128
QK_COLS = N_DGROUPS * N_HEADS * HEAD_DIM
V_COLS = N_HEADS * HEAD_DIM
ATTN_IN_COLS = 2 * QK_COLS + V_COLS

SSM_GROUP = 16
SSM_NGROUPS = D_MODEL // SSM_GROUP
SSM_STATE = 64
STEP_MIN = 0.001
STEP_MAX = 0.1

D_FF = 5632
CONV_W = 3

EPS = 1e-6

kernel_name = "hybrid_dilated_attn_s5_convffn_adaln"

def rms_norm(x, g):
    xf = x.astype(jnp.float32)
    y = xf * lax.rsqrt(jnp.mean(xf * xf, axis=-1, keepdims=True) + EPS)
    return (y * g.astype(jnp.float32)).astype(x.dtype)

def alibi_slopes():
    return 2.0 ** (-8.0 * jnp.arange(1, N_HEADS + 1, dtype=jnp.float32) / N_HEADS)

def dilated_branch(q, k, v, window, dilation):
    B, T, H, dh = q.shape
    blk = ATTN_BLOCK
    span = window // dilation
    L = -(-T // dilation)
    nb = -(-L // blk)
    Lp = nb * blk
    Tp = Lp * dilation

    def to_classes(a):
        a = jnp.pad(a, ((0, 0), (0, Tp - T), (0, 0), (0, 0)))
        a = a.reshape(B, Lp, dilation, H, dh).transpose(0, 2, 1, 3, 4)
        return a.reshape(B, dilation, nb, blk, H, dh)

    def with_prev(a):
        prev = jnp.pad(a, ((0, 0), (0, 0), (1, 0), (0, 0), (0, 0), (0, 0)))[:, :, :-1]
        return jnp.concatenate([prev, a], axis=3)

    qb = to_classes(q)
    kk = with_prev(to_classes(k))
    vv = with_prev(to_classes(v))

    s = jnp.einsum('brnqhc,brnkhc->brnhqk', qb, kk,
                   preferred_element_type=jnp.float32) * (HEAD_DIM ** -0.5)
    qi = jnp.arange(blk)[:, None]
    kj = jnp.arange(2 * blk)[None, :]
    dist = blk + qi - kj
    nidx = jnp.arange(nb)[:, None, None]
    valid = (dist >= 0) & (dist <= span) & (nidx * blk + kj - blk >= 0)
    bias = -alibi_slopes()[:, None, None] * (dist * dilation).astype(jnp.float32)
    s = jnp.where(valid[:, None], s + bias, -jnp.inf)
    m = jnp.max(s, axis=-1, keepdims=True)
    e = jnp.exp(s - m)
    den = jnp.sum(e, axis=-1, keepdims=True)
    lse = (m + jnp.log(den))[..., 0]
    p = e / den
    o = jnp.einsum('brnhqk,brnkhc->brnqhc', p, vv.astype(jnp.float32))
    o = o.reshape(B, dilation, Lp, H, dh).transpose(0, 2, 1, 3, 4).reshape(B, Tp, H, dh)[:, :T]
    lse = lse.transpose(0, 1, 2, 4, 3).reshape(B, dilation, Lp, H).transpose(0, 2, 1, 3)
    lse = lse.reshape(B, Tp, H)[:, :T]
    return o, lse

def dilated_attention(h, w_in, w_out):
    B, T, _ = h.shape
    proj = h @ w_in
    q, k, v = jnp.split(proj, [QK_COLS, 2 * QK_COLS], axis=-1)
    q = q.reshape(B, T, N_DGROUPS, N_HEADS, HEAD_DIM)
    k = k.reshape(B, T, N_DGROUPS, N_HEADS, HEAD_DIM)
    v = v.reshape(B, T, N_HEADS, HEAD_DIM)
    outs, lses = [], []
    for g, (window, dilation) in enumerate(DILATED_GROUPS):
        o, l = dilated_branch(q[:, :, g], k[:, :, g], v, window, dilation)
        outs.append(o)
        lses.append(l)
    wts = jax.nn.softmax(jnp.stack(lses, axis=0), axis=0)
    o = sum(wts[g][..., None] * outs[g] for g in range(N_DGROUPS))
    return o.reshape(B, T, V_COLS).astype(h.dtype) @ w_out

def _ssm_combine(left, right):
    a1r, a1i, b1r, b1i = left
    a2r, a2i, b2r, b2i = right
    return (a2r * a1r - a2i * a1i,
            a2r * a1i + a2i * a1r,
            a2r * b1r - a2i * b1i + b2r,
            a2r * b1i + a2i * b1r + b2i)

def _s5_core(ug, lb_re, lb_im, bb_re, bb_im, c_re, c_im):
    T = ug.shape[0]
    bu_re = jnp.einsum('tgc,gpc->tgp', ug, bb_re)
    bu_im = jnp.einsum('tgc,gpc->tgp', ug, bb_im)
    ar = jnp.broadcast_to(lb_re, (T,) + lb_re.shape)
    ai = jnp.broadcast_to(lb_im, (T,) + lb_im.shape)
    _, _, xr, xi = lax.associative_scan(_ssm_combine, (ar, ai, bu_re, bu_im), axis=0)
    return jnp.einsum('tgp,gcp->tgc', xr, c_re) - jnp.einsum('tgp,gcp->tgc', xi, c_im)

def s5_mixer(h, w_in, log_step, a_re, a_im, b_re, b_im, c_re, c_im, d_skip, w_gate, w_out):
    B, T, _ = h.shape
    f32 = jnp.float32
    u = (h @ w_in).astype(f32)
    ug = u.reshape(B, T, SSM_NGROUPS, SSM_GROUP)
    step = jnp.exp(log_step.astype(f32))[:, None]
    lr, li = a_re.astype(f32), a_im.astype(f32)
    mag = jnp.exp(lr * step)
    ang = li * step
    lb_re = mag * jnp.cos(ang)
    lb_im = mag * jnp.sin(ang)
    nr, ni = lb_re - 1.0, lb_im
    den = lr * lr + li * li
    coef_re = ((nr * lr + ni * li) / den)[..., None]
    coef_im = ((ni * lr - nr * li) / den)[..., None]
    br, bi = b_re.astype(f32), b_im.astype(f32)
    bb_re = coef_re * br - coef_im * bi
    bb_im = coef_re * bi + coef_im * br
    cr, ci = c_re.astype(f32), c_im.astype(f32)
    y = lax.map(lambda us: _s5_core(us, lb_re, lb_im, bb_re, bb_im, cr, ci), ug)
    y = y.reshape(B, T, D_MODEL) + d_skip.astype(f32) * u
    g = jax.nn.gelu(y).astype(h.dtype)
    g = g * jax.nn.sigmoid(g @ w_gate)
    return g @ w_out

def conv_ffn(h, w_up, conv_w, conv_b, w_down):
    T = h.shape[1]
    a = h @ w_up
    ap = jnp.pad(a, ((0, 0), (CONV_W - 1, 0), (0, 0)))
    a = conv_b + sum(conv_w[j] * ap[:, j:j + T] for j in range(CONV_W))
    gate, up = jnp.split(a, 2, axis=-1)
    return (jax.nn.silu(gate) * up) @ w_down

def setup_inputs(seed: int = 0) -> dict:
    key = jax.random.key(seed)
    ks = iter(jax.random.split(key, 32))
    f32 = jnp.float32

    def nrm(shape, std):
        return std * jax.random.normal(next(ks), shape, f32)

    D, F, G, P, C = D_MODEL, D_FF, SSM_NGROUPS, SSM_STATE, SSM_GROUP
    NA, NB = N_ATTN_LAYERS, N_SSM_LAYERS
    x = nrm((BATCH, SEQ, D), 1.0)
    c = nrm((BATCH, D), 1.0)
    ada_w = nrm((DEPTH, D, 6 * D), 0.3 * D ** -0.5)
    ada_b = nrm((DEPTH, 6 * D), 0.01)
    norm1_g = 1.0 + nrm((DEPTH, D), 0.05)
    norm2_g = 1.0 + nrm((DEPTH, D), 0.05)
    attn_w_in = nrm((NA, D, ATTN_IN_COLS), D ** -0.5)
    attn_w_out = nrm((NA, V_COLS, D), V_COLS ** -0.5)
    ssm_w_in = nrm((NB, D, D), D ** -0.5)
    ssm_log_step = jax.random.uniform(next(ks), (NB, G), f32,
                                      minval=math.log(STEP_MIN), maxval=math.log(STEP_MAX))
    ssm_a_re = -0.5 * jnp.exp(nrm((NB, G, P), 0.05))
    ssm_a_im = jnp.pi * jnp.arange(P, dtype=f32) + nrm((NB, G, P), 0.01)
    ssm_b_re = nrm((NB, G, P, C), (2.0 * C) ** -0.5)
    ssm_b_im = nrm((NB, G, P, C), (2.0 * C) ** -0.5)
    ssm_c_re = nrm((NB, G, C, P), P ** -0.5)
    ssm_c_im = nrm((NB, G, C, P), P ** -0.5)
    ssm_d = nrm((NB, D), 0.5)
    ssm_w_gate = nrm((NB, D, D), D ** -0.5)
    ssm_w_out = nrm((NB, D, D), D ** -0.5)
    ffn_w_up = nrm((DEPTH, D, 2 * F), D ** -0.5)
    ffn_conv_w = nrm((DEPTH, CONV_W, 2 * F), CONV_W ** -0.5)
    ffn_conv_b = nrm((DEPTH, 2 * F), 0.01)
    ffn_w_down = nrm((DEPTH, F, D), F ** -0.5)
    final_norm_g = 1.0 + nrm((D,), 0.05)
    return {"x": x, "c": c, "ada_w": ada_w, "ada_b": ada_b,
            "norm1_g": norm1_g, "norm2_g": norm2_g,
            "attn_w_in": attn_w_in, "attn_w_out": attn_w_out,
            "ssm_w_in": ssm_w_in, "ssm_log_step": ssm_log_step,
            "ssm_a_re": ssm_a_re, "ssm_a_im": ssm_a_im,
            "ssm_b_re": ssm_b_re, "ssm_b_im": ssm_b_im,
            "ssm_c_re": ssm_c_re, "ssm_c_im": ssm_c_im,
            "ssm_d": ssm_d, "ssm_w_gate": ssm_w_gate, "ssm_w_out": ssm_w_out,
            "ffn_w_up": ffn_w_up, "ffn_conv_w": ffn_conv_w, "ffn_conv_b": ffn_conv_b,
            "ffn_w_down": ffn_w_down, "final_norm_g": final_norm_g}

def reference(x, c, ada_w, ada_b, norm1_g, norm2_g, attn_w_in, attn_w_out,
              ssm_w_in, ssm_log_step, ssm_a_re, ssm_a_im, ssm_b_re, ssm_b_im,
              ssm_c_re, ssm_c_im, ssm_d, ssm_w_gate, ssm_w_out,
              ffn_w_up, ffn_conv_w, ffn_conv_b, ffn_w_down, final_norm_g):
    cs = jax.nn.silu(c)
    for i in range(DEPTH):
        j = i // N_MIXERS
        mod = (cs @ ada_w[i] + ada_b[i])[:, None, :]
        sh1, sc1, g1, sh2, sc2, g2 = jnp.split(mod, 6, axis=-1)
        h = rms_norm(x, norm1_g[i]) * (1.0 + sc1) + sh1
        if i % N_MIXERS == 0:
            mix = dilated_attention(h, attn_w_in[j], attn_w_out[j])
        else:
            mix = s5_mixer(h, ssm_w_in[j], ssm_log_step[j], ssm_a_re[j], ssm_a_im[j],
                           ssm_b_re[j], ssm_b_im[j], ssm_c_re[j], ssm_c_im[j],
                           ssm_d[j], ssm_w_gate[j], ssm_w_out[j])
        x = x + g1 * mix
        h = rms_norm(x, norm2_g[i]) * (1.0 + sc2) + sh2
        x = x + g2 * conv_ffn(h, ffn_w_up[i], ffn_conv_w[i], ffn_conv_b[i], ffn_w_down[i])
    return rms_norm(x, final_norm_g)


_drawn_inputs = setup_inputs


def setup_inputs(seed=0):
    import zlib

    import numpy as np

    out = dict(_drawn_inputs(seed))
    spreads = {}
    factors = {'ada_b': 5.044,
     'norm1_g': 8.0,
     'norm2_g': 4.524,
     'ssm_log_step': 64.0,
     'ssm_a_re': 64.0,
     'ssm_a_im': 64.0,
     'ssm_b_re': 64.0,
     'ssm_b_im': 64.0,
     'ssm_c_re': 64.0,
     'ssm_c_im': 64.0,
     'ssm_w_gate': 8.0,
     'ffn_conv_b': 8.0}
    for name, (base, spread) in spreads.items():
        noise = np.random.default_rng([zlib.crc32(name.encode()), seed]).standard_normal(out[name].shape)
        drawn = base * np.exp(spread * noise) if base else spread * noise
        out[name] = __import__('jax').numpy.asarray(drawn.astype(out[name].dtype))
    for name, factor in factors.items():
        out[name] = (out[name] * factor).astype(out[name].dtype)
    return out
```

```python
import math
from contextlib import ExitStack

import numpy as np

import concourse.bass as bass
from concourse import mybir

F32 = mybir.dt.float32
F32R = mybir.dt.float32r
I32 = mybir.dt.int32
ALU = mybir.AluOpType
ACT = mybir.ActivationFunctionType
AX = mybir.AxisListType

P = 128
D = 2048
T = 256
KT = D // P
HEADS = 16
GROUPS = ((128, 1), (512, 4), (2048, 16))
NG = len(GROUPS)
SCALE = P ** -0.5
F = 5632
FB = F // P
HALF = FB // 2
EPS = 1e-6
SG, SC, SP_ = 128, 16, 64
TILES = SG * SP_ // P
NEG = -1e30

PIECE = 8
HI_FIRST, LO_FIRST = 4, 2
LAG = 4
RAW = 8
S5_RAW = 4
MODW = 1024
MODB = MODW // P
ADA = 4
TABS = 8


class Stream:

    def __init__(self, name, base, blocks_before, slots, uses, count, pieces, ring, tight, ada):
        self.base, self.block0, self.count, self.pieces = base, blocks_before, count, pieces
        self.name, self.ring, self.tight, self.slots, self.ada = name, ring, tight, slots, ada
        self.length = len(pieces)
        self.blocks = pieces[-1][0] + 1
        self.uses = list(uses)
        assert self.length % ring == 0 and self.length % LAG == 0 and base % LAG == 0
        assert self.blocks % 2 == 0 and blocks_before % 2 == 0
        self.end_of = [max(j for j, p in enumerate(pieces) if p[0] == b) for b in range(self.blocks)]

    def number(self, i, j):
        return self.base + i * self.length + j

    def block(self, i, b):
        return self.block0 + i * self.blocks + b

    def landed(self, i, j):
        return (i * (self.length // self.ring) + self.uses[j % self.ring] + j // self.ring + 1) * 16


def plan():
    streams, uses, base, blocks = {}, [0] * RAW, 0, 0
    last_ring = RAW
    two = [(0, PIECE, False), (PIECE, PIECE, True)]
    down = [(0, 8, False), (8, 7, False), (15, 7, True)]

    def add(name, count, nblocks, parts, ring=RAW, ada=None):
        nonlocal base, blocks, last_ring
        pieces = [(b, *p) for b in range(nblocks) for p in parts]
        s = Stream(name, base, blocks, None, uses, count, pieces, ring, min(ring, last_ring), ada)
        streams[name] = s
        base += count * s.length
        blocks += count * s.blocks
        for j in range(ring):
            uses[j] += count * (s.length // ring)
        last_ring = ring
        return s

    spread = lambda n, steps: {s: [k for k in range(n) if k * steps // n == s] for s in range(steps)}
    add("qkv", 8, 14, two, ring=7, ada=(0, 4, spread(16, 24)))
    add("attn_out", 1, 16, two, ada=(1, 0, spread(16, 28)))
    add("up0a", 3, 12, two, ada=(1, 1, spread(16, 21)))
    add("up0a_end", 1, 8, two, ada=(1, 4, spread(16, 13)))
    add("down0a", 2, 8, down, ada=(1, 5, spread(16, 21)))
    add("up0b", 3, 12, two, ada=(1, 7, spread(16, 21)))
    add("up0b_end", 1, 8, two)
    add("down0b", 2, 8, down, ada=(1, 10, spread(16, 21)))
    add("ssm_in", 4, 4, two, ring=S5_RAW)
    add("gate", 4, 4, two, ring=S5_RAW)
    add("ssm_out", 4, 4, two)
    for h in "ab":
        add("up1" + h, 5, 8, two)
        add(f"up1{h}_end", 1, 4, two)
        add("down1" + h, 2, 8, down)
    return streams


def run_steps(eng, count, length, step, late, peel_last=False, done=0):

    def body(i, first):
        for j in range(length):
            if not first or j >= done:
                step(i, j)
            if not first:
                for f in late.get(j + length, ()):
                    f(i - 1)
            for f in late.get(j, ()):
                f(i)

    body(0, True)
    if count - peel_last > 1:
        with eng.Fori(1, count - peel_last) as i:
            body(i, False)
    if peel_last:
        body(count - 1, False)
    for due in sorted(late):
        if due >= length:
            for f in late[due]:
                f(count - 1)


def wait(eng, sem, value):
    if not isinstance(value, int) or value > 0:
        eng.wait_ge(sem, value)


def build(nc, a, out):
    st = plan()
    ctx = ExitStack()
    with ctx:
        def sb(name, shape, dt=F32):
            return ctx.enter_context(nc.sbuf_tensor(name, [P, *shape], dt))

        def bank(name, shape):
            return ctx.enter_context(nc.psum_tensor(name, [P, *shape], F32))

        def sem(name):
            return ctx.enter_context(nc.semaphore(name))

        h_hi, h_lo = sb("h_hi", [KT, T], F32R), sb("h_lo", [KT, T], F32R)
        a_hi, a_lo = sb("a_hi", [HALF, T], F32R), sb("a_lo", [HALF, T], F32R)
        w_hi, w_lo = sb("w_hi", [LAG, PIECE * P], F32R), sb("w_lo", [LAG, PIECE * P], F32R)
        x = sb("x", [KT, T])
        raw = sb("raw", [RAW, PIECE * P])
        ada = sb("ada", [ADA, MODW])
        acc = sb("acc", [MODW])
        work = sb("work", [5888])
        ident = sb("ident", [P])
        mean_w = sb("mean_w", [P])
        rstd = sb("rstd", [T])
        meansq, newton = sb("meansq", [T])[:], sb("newton", [T])[:]
        square = sb("square", [T])
        sumsq = sb("sumsq", [T])
        mod = sb("mod", [2, 12 * MODB])
        mod_b = sb("mod_b", [2, 12 * MODB])
        gains = sb("gains", [5, KT])
        hscale = sb("hscale", [KT])
        cs = sb("cs", [KT])
        slopes = sb("slopes", [HEADS])
        ones = sb("ones", [2])
        halves = sb("halves", [4])
        small = sb("small", [8])
        dskip = sb("dskip", [KT])
        mag = sb("mag", [TILES])

        def cut(region, offset, *shape):
            n = int(np.prod(shape))
            v = region[:, offset:offset + n]
            if len(shape) == 2:
                v = v.rearrange("p (a b) -> p a b", a=shape[0])
            if len(shape) == 3:
                v = v.rearrange("p (a b c) -> p a b c", a=shape[0], b=shape[1])
            if len(shape) == 4:
                v = v.rearrange("p (a b c d) -> p a b c d", a=shape[0], b=shape[1], c=shape[2])
            return v, offset + n

        raw_flat = raw[:, :, :].rearrange("p a b -> p (a b)")
        ef, o = cut(raw_flat, 0, TILES, 6, 16)
        c_raw, o = cut(raw_flat, o, TILES, 2, SC)
        acc2, o = cut(work, 0, MODW)
        t16, _ = cut(work, o, TILES, 16)
        t8a, o = cut(work, o, TILES, 8)
        t8b, o = cut(work, o, TILES, 8)
        c_new, o = cut(work, o, TILES, 2, SC)
        prep, o = cut(work, o, 14, TILES)
        hf, o = cut(work, 0, 2, 4, T)
        qk, o = cut(work, 0, 2, 6, T)
        v_t, o = cut(work, o, T)
        v_sb, o = cut(work, o, 2, P)
        rel, o = cut(work, o, NG, T)
        s0, o = cut(work, o, NG, P)
        s1, o = cut(work, o, NG, T)
        p_t, o = cut(work, o, 3 * P)
        taps, o = cut(work, 2048, FB, 2, 3)
        tap_b, o = cut(work, o, FB, 2)
        conv, o = cut(work, 2400, 2, 2, T)
        silu, o = cut(work, o, 2, T)
        gated, o = cut(work, o, 2, T)
        ef_in, o = cut(work, 2400, 4, 6, 16)
        tab_a, o = cut(work, o, 2, 16, 16)
        tab_b, o = cut(work, o, 2, 16, 16)
        tab_o, o = cut(work, 4448, 2, 512)
        bu, o = cut(work, 0, 2, 3, T)
        z, o = cut(work, o, 2, 2, T)
        xs, o = cut(work, o, 2, 4, T)
        c_wide, o = cut(work, o, 2, 4, 3, 2 * SC)
        ada_flat = ada[:, :, :].rearrange("p a b -> p (a b)")
        tabs4, o = cut(ada_flat, 0, 4, 2, T)
        more_tabs, o_raw = cut(raw_flat, S5_RAW * PIECE * P, 4, 2, T)
        tabs = [v[:, q] for v in (tabs4, more_tabs) for q in range(4)]
        zin, o_raw = cut(raw_flat, o_raw, 2, 2, T)
        zin2, _ = cut(raw_flat, o_raw, 2, 2, T)
        c_cur, o = cut(ada_flat, o, 2, 4, 2, SC)
        b_cur, o = cut(ada_flat, o, 2, 2, SP_)
        b_wide, o = cut(ada_flat, o, 2, 2, P)
        u, o = cut(ada_flat, o, 4, T)
        ypre, _ = cut(acc[:, :], 0, 2, T)
        geluo, _ = cut(acc[:, :], 512, 2, T)
        gfull, o = cut(work, 0, 2, T)
        sig, o = cut(work, o, 2, T)
        gmul, o = cut(work, o, 2, T)

        proj = [bank("proj0", [512]), bank("proj1", [512])]
        ps1 = bank("ps1", [1024])
        ps0 = bank("ps0", [512])
        pturn = bank("pturn", [512])
        pmisc = bank("pmisc", [512])
        pout = bank("pout", [512])
        mod_ps = pmisc[:, 256:256 + MODB]
        norm_ps = pout[:, 0:T]
        bu_ps = [ps1[:, 0:512], ps1[:, 512:1024], pturn, pout]
        y_ps = [ps0, pmisc]

        ef_d = nc.dram_tensor("ef_d", [TILES, P, 96], F32, kind="Internal").ap()
        tab_d = nc.dram_tensor("tab_d", [TILES, P, 512], F32, kind="Internal").ap()
        cw_d = nc.dram_tensor("cw_d", [P, TILES, 2 * SC], F32, kind="Internal").ap()

        consts_in, ones_ready = sem("consts_in"), sem("ones_ready")
        x_in, root_ready = sem("x_in"), sem("root_ready")
        raw_in = [sem(f"raw_in{s}") for s in range(RAW)]
        ada_in = [sem(f"ada_in{s}") for s in range(ADA)]
        hi_ready, lo_ready, piece_done, block_out = sem("hi_ready"), sem("lo_ready"), sem("piece_done"), sem("block_out")
        cs_ready = sem("cs_ready")
        ada_scaled, ada_added, ada_used = sem("ada_scaled"), sem("ada_added"), sem("ada_used")
        mod_summed, mod_ready = sem("mod_summed"), sem("mod_ready")
        prep_link, prep_done = sem("prep_link"), sem("prep_done")
        ef_out, cw_out = sem("ef_out"), sem("cw_out")
        sq_made, sumsq_made, mean_ready = sem("sq_made"), sem("sumsq_made"), sem("mean_ready")
        norm_link, norm_full, norm_hi, norm_lo = sem("norm_link"), sem("norm_full"), sem("norm_hi"), sem("norm_lo")
        scores_done, v_turned, s_biased, max_found, max_ready = (
            sem("scores_done"), sem("v_turned"), sem("s_biased"), sem("max_found"), sem("max_ready"))
        exp_done, v_ready, rden_ready, mix_link, mix_ready = (
            sem("exp_done"), sem("v_ready"), sem("rden_ready"), sem("mix_link"), sem("mix_ready"))
        p_turned, p_copied, pv_done, o_hi, o_lo = (
            sem("p_turned"), sem("p_copied"), sem("pv_done"), sem("o_hi"), sem("o_lo"))
        rel_in = sem("rel_in")
        taps_in = sem("taps_in")
        conv0, conv1, silu_ready, gated_ready, act_hi, act_lo = (
            sem("conv0"), sem("conv1"), sem("silu_ready"), sem("gated_ready"), sem("act_hi"), sem("act_lo"))
        ef_in_s = [sem("ef_in_s0"), sem("ef_in_s1")]
        tab_link, tab_made, y_tile = sem("tab_link"), sem("tab_made"), sem("y_tile")
        tab_out = [sem("tab_out0"), sem("tab_out1")]
        tabs_in = [sem(f"tabs_in{q}") for q in range(TABS)]
        bc_in = [sem("bc_in0"), sem("bc_in1")]
        cc_in = [sem("cc_in0"), sem("cc_in1")]
        c_made = sem("c_made")
        b_made, bu_done, bu_copied, rot_done, zin_added, scanned, xs_done = (
            sem("b_made"), sem("bu_done"), sem("bu_copied"), sem("rot_done"), sem("zin_added"),
            sem("scanned"), sem("xs_done"))
        ypre_done, gelu_done, g_hi, g_lo = (
            sem("ypre_done"), sem("gelu_done"), sem("g_hi"), sem("g_lo"))
        gf_ready, gm_ready, gg_hi, gg_lo = (
            sem("gf_ready"), sem("gm_ready"), sem("gg_hi"), sem("gg_lo"))
        out_ready, out_done = sem("out_ready"), [sem("out_done0"), sem("out_done1")]

        UPS = {"up0a": 0, "up0a_end": 18, "up0b": 22, "up0b_end": 40,
               "up1a": 44, "up1a_end": 64, "up1b": 66, "up1b_end": 86}
        TAB0 = {"attn_out": 0, "down0a": 16, "down0b": 40}
        TAB_EVERY = 2

        def ada_part_done(name):
            n = 4
            for s in st.values():
                if s.name == name:
                    return n
                n += s.count if s.ada else 0
            return n

        block = ctx.enter_context(nc.Block())

        @block.sync
        def _(sp):
            for dst, src in ((cs, a["c"]), (ident, a["ident"]), (mean_w, a["mean_w"]), (mod_b, a["ada_b"]),
                             (gains, a["gains"]), (slopes, a["slopes"]), (halves, a["halves"]),
                             (dskip, a["ssm_d"]), (prep[:, 0:3, :], a["ssm_p"])):
                sp.dma_start(dst if dst is prep else dst[:], src).then_inc(consts_in, 16)
            sp.dma_start(c_raw, a["ssm_c"]).then_inc(consts_in, 16)

            for n in range(64):
                if n >= ADA:
                    used = ada_added if n % 2 == 0 else ada_used
                    sp.wait_ge(used, (n - ADA) // 2 + 1)
                m = n // 2
                sp.dma_start(ada[:, n % ADA, :], a["ada_w"][0, m % KT, 2 * (n % 2) + m // KT]).then_inc(
                    ada_in[n % ADA], 16)
                if n == 8:
                    sp.dma_start(x[:], a["x"]).then_inc(x_in, 16)
            sp.wait_ge(prep_done, 1)
            sp.dma_start(ef_d.rearrange("t p n -> p t n"), ef.rearrange("p t a b -> p t (a b)")).then_inc(ef_out, 16)
            sp.dma_start(cw_d, c_new.rearrange("p t a b -> p t (a b)")).then_inc(cw_out, 16)
            sp.wait_ge(ef_out, 16)

            def weights(name, src):
                s = st[name]

                def load(i, j):
                    blk, k0, nk, _ = s.pieces[j]
                    n = s.number(i, j)
                    ahead = s.tight if isinstance(i, int) else s.ring
                    wait(sp, lo_ready, n - ahead + 1)
                    sp.dma_start(raw[:, j % s.ring, 0:nk * P], src(i, blk)[:, k0 * P:(k0 + nk) * P]).then_inc(
                        raw_in[j % s.ring], 16)
                    if s.ada:
                        layer, part0, when = s.ada
                        for k in when.get(j, ()):
                            if isinstance(n, int) and s.base + j == 0 and k == 0:
                                sp.wait_ge(ada_added, 2 * KT)
                                sp.wait_ge(ada_used, 2 * KT)
                            part = ada_part_done(name) + i
                            sp.wait_ge(ada_used, 32 + KT * (part - 4) + k - ADA + 1)
                            sp.dma_start(ada[:, k % ADA, :], a["ada_w"][layer, k, i + part0]).then_inc(
                                ada_in[k % ADA], 16)

                run_steps(sp, s.count, s.length, load, {})

            def ffn(layer):
                w = a["w_up"][layer]
                d = a["w_down"][layer]
                for half, h in enumerate("ab"):
                    u0 = 22 * half
                    n = st[f"up{layer}{h}"]
                    pairs = n.blocks // 2
                    weights(f"up{layer}{h}", lambda i, b: w[u0 + pairs * i + b // 2, b % 2])
                    done = u0 + pairs * n.count
                    weights(f"up{layer}{h}_end", lambda i, b: w[done + b // 2, b % 2])
                    weights(f"down{layer}{h}", lambda i, b: d[half, 8 * i + b])

            weights("qkv", lambda i, b: a["w_in"][2 * i + b // 7, b % 7])
            weights("attn_out", lambda i, b: a["w_out"][b])
            ffn(0)
            weights("ssm_in", lambda i, b: a["ssm_w_in"][4 * i + b])
            weights("gate", lambda i, b: a["ssm_w_gate"][4 * i + b])
            weights("ssm_out", lambda i, b: a["ssm_w_out"][4 * i + b])
            ffn(1)
            for q in range(4):
                sp.wait_ge(out_ready, 4 * q + 4)
                sp.dma_start(out[:, 4 * q:4 * q + 4, :], hf[:, q % 2]).then_inc(out_done[q % 2], 16)
            for q in range(2):
                sp.wait_ge(out_done[q], 32)

        @block.scalar
        def _(act):
            act.wait_ge(consts_in, 16 * 10)
            nc.scalar.activation(cs[:], cs[:], ACT.Silu).then_inc(cs_ready, 1)

            def high(s):
                def f(i, j):
                    _, _, nk, _ = s.pieces[j]
                    act.wait_ge(raw_in[j % s.ring], s.landed(i, j))
                    wait(act, piece_done, s.number(i, j) - LAG + 1)
                    nc.scalar.activation(w_hi[:, j % LAG, 0:nk * P], raw[:, j % s.ring, 0:nk * P],
                                         ACT.Copy).then_inc(hi_ready, 1)
                return f

            def split_first(name):
                for j in range(HI_FIRST):
                    high(st[name])(0, j)

            def root(number):
                act.wait_ge(norm_link, 10 * number + 2)
                nc.scalar.activation(rstd[:], meansq, ACT.Sqrt).then_inc(root_ready, 1)

            def norm(number):
                root(number)
                for q in range(4):
                    act.wait_ge(norm_full, 16 * number + 4 * q + 4)
                    nc.scalar.activation(h_hi[:, 4 * q:4 * q + 4, :], hf[:, q % 2], ACT.Copy).then_inc(norm_hi, 1)

            def block_ready(s, i, b):
                act.wait_ge(piece_done, s.number(i, s.end_of[b]) + 1)

            for m in range(2 * KT):
                n = 2 * m
                act.wait_ge(ada_in[n % ADA], 16 * (n // ADA + 1))
                if m == 0:
                    act.wait_ge(cs_ready, 1)
                nc.scalar.activation(ada[:, n % ADA, :], ada[:, n % ADA, :], ACT.Copy,
                                     scale=cs[:, m % KT:m % KT + 1]).then_inc(ada_scaled, 1)
            norm(0)
            act.wait_ge(norm_lo, 4)
            act.wait_ge(cw_out, 16)
            act.dma_start(rel, a["rel"]).then_inc(rel_in, 16)
            s = st["qkv"]
            late = {}

            def evacuate(hl, m):
                def f(i):
                    head = 2 * i + hl
                    if m < 6:
                        wait(act, scores_done, head if (hl, m) == (1, 5) else head - 1)
                        dst = qk[:, hl, m, :]
                    else:
                        wait(act, v_turned, head)
                        dst = v_t
                    block_ready(s, i, 7 * hl + m)
                    nc.scalar.activation(dst, proj[(7 * hl + m) % 2][:, 0:T], ACT.Copy).then_inc(block_out, 1)
                return f

            def exponentials(hl):
                def f(i):
                    head = 2 * i + hl
                    act.wait_ge(max_ready, head + 1)
                    nc.scalar.activation(s0, s0, ACT.Exp, bias=small[:, 2:3], scale=SCALE,
                                         accum_out=small[:, 4:5]).then_inc(exp_done, 1)
                    nc.scalar.activation(s1, s1, ACT.Exp, bias=small[:, 3:4], scale=SCALE,
                                         accum_out=small[:, 5:6]).then_inc(exp_done, 1)
                    act.wait_ge(v_turned, head + 1)
                    wait(act, pv_done, head)
                    nc.scalar.activation(v_sb, pmisc[:, 0:2 * P].rearrange("p (a b) -> p a b", a=2),
                                         ACT.Copy).then_inc(v_ready, 1)
                return f

            def copy_p(hl):
                def f(i):
                    head = 2 * i + hl
                    act.wait_ge(p_turned, head + 1)
                    wait(act, pv_done, head)
                    nc.scalar.activation(p_t, pturn[:, 0:3 * P],
                                         ACT.Copy).then_inc(p_copied, 1)
                return f

            def out_high(hl):
                def f(i):
                    head = 2 * i + hl
                    act.wait_ge(pv_done, head + 1)
                    nc.scalar.activation(a_hi[:, head, :], pout[:, 0:T], ACT.Copy).then_inc(o_hi, 1)
                return f

            for hl in range(2):
                for m in range(7):
                    late.setdefault(14 * hl + 2 * m + 5, []).append(evacuate(hl, m))
                late.setdefault(14 * hl + 14 + 9, []).append(exponentials(hl))
                late.setdefault(14 * hl + 14 + 13, []).append(copy_p(hl))
                late.setdefault(14 * hl + 14 + 18, []).append(out_high(hl))
            run_steps(act, s.count, s.length, high(s), late)

            def plain(name):
                s = st[name]
                late = {}
                if name in TAB0:
                    per = s.length // TAB_EVERY

                    def factors(q):
                        def f(i):
                            t0 = TAB0[name] + i * per + q
                            if isinstance(i, int) and q == 0 and name != "attn_out":
                                act.wait_ge(act_lo, HALF if name == "down0a" else FB)
                            wait(act, tab_link, 2 * t0)
                            act.dma_start(ef_in[:, 0:4], ef_d[bass.ds(t0, 4)].rearrange("t p (a b) -> p t a b", b=16)
                                          ).then_inc(ef_in_s[0], 16)
                        return f

                    def store(q):
                        def f(i):
                            t = TAB0[name] + i * per + q
                            act.wait_ge(tab_made, t + 1)
                            act.dma_start(tab_d[t], tab_o[:, q % 2, :]).then_inc(tab_out[q % 2], 16)
                        return f
                    for q in range(per):
                        if q % 4 == 0:
                            late.setdefault(TAB_EVERY * q + 4, []).append(factors(q))
                        late.setdefault(TAB_EVERY * q + 7, []).append(store(q))
                run_steps(act, s.count, s.length, high(s), late)

            def up(name, layer):
                s = st[name]
                pair0 = UPS[name]
                f0 = pair0 - 44 * layer

                def tap2(pl, side):
                    def f(i):
                        pair = pair0 + i * (s.blocks // 2) + pl
                        fb = f0 + i * (s.blocks // 2) + pl
                        block_ready(s, i, 2 * pl + side)
                        wait(act, gated_ready, pair - 1)
                        nc.scalar.activation(conv[:, pl % 2, side, :], proj[side][:, 0:T], ACT.Identity,
                                             bias=tap_b[:, fb, side:side + 1],
                                             scale=taps[:, fb, side, 2:3]).then_inc(conv0, 1)
                        if side == 1:
                            act.wait_ge(block_out, s.block(i, 2 * pl) + 1)
                            nc.scalar.activation(silu[:, pl % 2, :], conv[:, pl % 2, 0, :], ACT.Silu).then_inc(silu_ready, 1)
                    return f

                def act_high(pl):
                    def f(i):
                        pair = pair0 + i * (s.blocks // 2) + pl
                        dst = pair0 % HALF + i * (s.blocks // 2) + pl
                        act.wait_ge(gated_ready, pair + 1)
                        nc.scalar.activation(a_hi[:, dst, :], gated[:, pl % 2, :], ACT.Copy).then_inc(act_hi, 1)
                    return f

                late = {}
                for pl in range(s.blocks // 2):
                    late.setdefault(4 * pl + 5, []).append(tap2(pl, 0))
                    late.setdefault(4 * pl + 7, []).append(tap2(pl, 1))
                    late.setdefault(4 * pl + 9, []).append(act_high(pl))
                run_steps(act, s.count, s.length, high(s), late,
                          done=HI_FIRST * (name in ("up0a", "up1a")))

            def load_taps(layer):
                act.dma_start(taps, a["conv_w"][layer]).then_inc(taps_in, 16)
                act.dma_start(tap_b, a["conv_b"][layer]).then_inc(taps_in, 16)

            def ffn(layer):
                act.wait_ge(taps_in, 32 * (layer + 1))
                for h in "ab":
                    up(f"up{layer}{h}", layer)
                    up(f"up{layer}{h}_end", layer)
                    plain(f"down{layer}{h}")

            act.wait_ge(o_lo, HEADS)
            act.wait_ge(pv_done, HEADS)
            load_taps(0)
            act.wait_ge(ef_out, 16)
            plain("attn_out")
            split_first("up0a")
            norm(1)
            ffn(0)
            split_first("ssm_in")
            norm(2)
            for q in range(2):
                act.wait_ge(tab_out[q], 16 * TILES // 2)
            act.wait_ge(mod_ready, 24)

            def load_table(t, q):
                wait(act, xs_done, 2 * (t - TABS + 1))
                act.dma_start(tabs[q], tab_d[t].rearrange("p (a b) -> p a b", a=2)).then_inc(tabs_in[q], 16)

            def load_b(n, b):
                wait(act, b_made, n - 1)
                act.dma_start(b_cur[:, b], a["ssm_b"][n]).then_inc(bc_in[b], 16)

            def load_c(n, b):
                wait(act, c_made, n - 1)
                act.dma_start(c_cur[:, b], cw_d[:, bass.ds(n * 4, 4), :].rearrange("p t (a b) -> p t a b", a=2)
                              ).then_inc(cc_in[b], 16)

            for n in range(2):
                load_b(n, n)
                load_c(n, n)
            for t in range(TABS - 4):
                load_table(t, t)
            s = st["ssm_in"]
            late = {}

            def take_u(b):
                def f(i):
                    n = 4 * i + b
                    block_ready(s, i, b)
                    if b < 2:
                        wait(act, ypre_done, n - 3)
                    nc.scalar.activation(u[:, b, :], proj[b % 2][:, 0:T], ACT.Copy).then_inc(block_out, 1)
                    if b < 2 or not isinstance(i, int) or i < s.count - 1:
                        load_b(n + 2, b % 2)
                return f

            def take_bu(tl):
                def f(i):
                    t = 16 * i + tl
                    act.wait_ge(bu_done, t + 1)
                    wait(act, rot_done, 2 * (t - 1))
                    if tl == 2:
                        wait(act, g_lo, 4 * i - 1)
                    nc.scalar.activation(bu[:, tl % 2, 0:2, :], bu_ps[tl % 4][:, :].rearrange("p (a b) -> p a b", a=2),
                                         ACT.Copy).then_inc(bu_copied, 1)
                    nc.scalar.activation(bu[:, tl % 2, 2, :], bu_ps[tl % 4][:, 0:T],
                                         ACT.Copy, scale=-1.0).then_inc(bu_copied, 1)
                    if tl < 12 or not isinstance(i, int) or i < s.count - 1:
                        load_table(t + 4, (tl + 4) % TABS)
                    if tl % 4 == 2 and (tl < 8 or not isinstance(i, int) or i < s.count - 1):
                        load_c(4 * i + tl // 4 + 2, tl // 4 % 2)
                return f

            def gelu(b):
                def f(i):
                    n = 4 * i + b
                    act.wait_ge(ypre_done, n + 1)
                    if b:
                        act.wait_ge(g_lo, n)
                    nc.scalar.activation(geluo[:, b % 2, :], ypre[:, b % 2, :], ACT.Gelu_apprx_tanh).then_inc(gelu_done, 1)
                    act.wait_ge(gelu_done, n + 1)
                    nc.scalar.activation(a_hi[:, n, :], geluo[:, b % 2, :], ACT.Copy).then_inc(g_hi, 1)
                return f
            for b in range(4):
                late.setdefault(2 * b + 5, []).append(take_u(b))
                for q in range(4):
                    late.setdefault(2 * b + 6 + q // 2, []).append(take_bu(4 * b + q))
                late.setdefault(min(2 * b + 10, 15), []).append(gelu(b))
            run_steps(act, s.count, s.length, high(s), late, peel_last=True, done=HI_FIRST)
            s = st["gate"]
            late = {}

            def gate(b):
                def f(i):
                    n = 4 * i + b
                    block_ready(s, i, b)
                    wait(act, gm_ready, n - 1)
                    nc.scalar.activation(sig[:, b % 2, :], proj[b % 2][:, 0:T], ACT.Sigmoid).then_inc(block_out, 1)
                return f

            def gate_high(b):
                def f(i):
                    n = 4 * i + b
                    act.wait_ge(gm_ready, n + 1)
                    nc.scalar.activation(h_hi[:, n, :], gmul[:, b % 2, :], ACT.Copy).then_inc(gg_hi, 1)
                return f
            for b in range(4):
                late.setdefault(2 * b + 5, []).append(gate(b))
                late.setdefault(2 * b + 7, []).append(gate_high(b))
            run_steps(act, s.count, s.length, high(s), late)
            act.wait_ge(gg_lo, KT)
            load_taps(1)
            plain("ssm_out")
            split_first("up1a")
            norm(3)
            ffn(1)
            root(4)

        @block.vector
        def _(dve):
            V = nc.vector
            links, adds = [0], [0]

            def link(ins):
                links[0] += 1
                ins.then_inc(prep_link, 1)
                if links[0] > 20 and links[0] % 6 == 0 and adds[0] < 2 * KT:
                    ada_add(adds[0])
                dve.wait_ge(prep_link, links[0])

            def exp_small(dst, src, k, r, q):
                magic = 12582912.0
                link(V.tensor_scalar(r, src, -88.2, 89.0, ALU.max, ALU.min))
                link(V.tensor_scalar(k, r, 1.0 / math.log(2.0), magic, ALU.mult, ALU.add))
                link(V.tensor_scalar(k, k, magic, None, ALU.subtract))
                link(V.scalar_tensor_tensor(out=r, in0=k, scalar=-0.693359375, in1=r, op0=ALU.mult, op1=ALU.add))
                link(V.scalar_tensor_tensor(out=r, in0=k, scalar=2.12194440e-4, in1=r, op0=ALU.mult, op1=ALU.add))
                link(V.tensor_scalar(q, r, 1.0 / math.factorial(8), None, ALU.mult))
                for n in range(7, 0, -1):
                    link(V.scalar_tensor_tensor(out=q, in0=q, scalar=1.0 / math.factorial(n), in1=r,
                                                op0=ALU.add, op1=ALU.mult))
                link(V.tensor_scalar(k, k, 127.0 + 8388608.0, None, ALU.add))
                link(V.tensor_single_scalar(k.bitcast(I32), k.bitcast(I32), 23, ALU.logical_shift_left))
                link(V.scalar_tensor_tensor(out=dst, in0=q, scalar=1.0, in1=k, op0=ALU.add, op1=ALU.mult))

            def add_piece(slot, k, done):
                c = cs[:, k:k + 1]
                if k == 0:
                    V.tensor_scalar(acc[:], ada[:, slot, :], c, None, ALU.mult).then_inc(ada_used, 1)
                else:
                    dve.wait_ge(ada_used, done)
                    V.scalar_tensor_tensor(out=acc[:], in0=ada[:, slot, :], scalar=c, in1=acc[:],
                                           op0=ALU.mult, op1=ALU.add).then_inc(ada_used, 1)

            def ada_add(m):
                adds[0] += 1
                n = 2 * m + 1
                if m == 0:
                    dve.wait_ge(cs_ready, 1)
                if m == KT:
                    take_mod(0, 0, 1)
                    take_mod(0, 2, 2)
                dve.wait_ge(ada_in[n % ADA], 16 * (n // ADA + 1))
                add_piece(n % ADA, m % KT, m)

            def take_mod(layer, part, done):
                dve.wait_ge(mod_summed, done)
                cols = bass.ds(part * MODB, MODB)
                V.tensor_tensor(mod[:, layer, cols], mod_ps, mod_b[:, layer, cols], ALU.add).then_inc(mod_ready, 1)

            def low(s):
                def f(i, j):
                    _, _, nk, _ = s.pieces[j]
                    dve.wait_ge(hi_ready, s.number(i, j) + 1)
                    V.tensor_tensor(w_lo[:, j % LAG, 0:nk * P], raw[:, j % s.ring, 0:nk * P],
                                    w_hi[:, j % LAG, 0:nk * P].bitcast(F32), ALU.subtract).then_inc(lo_ready, 1)
                    if s.ada:
                        part = ada_part_done(s.name) + i
                        for k in s.ada[2].get(j, ()):
                            if k == 0:
                                dve.wait_ge(mod_summed, part)
                            dve.wait_ge(ada_in[k % ADA], 16 * (16 + 4 * (part - 4) + k // ADA + 1))
                            add_piece(k % ADA, k, 2 * KT + KT * (part - 4) + k)
                return f

            def split_first(name):
                for j in range(LO_FIRST):
                    low(st[name])(0, j)

            def take_parts(s, late):
                if s.ada:
                    layer, part0, _ = s.ada
                    before = ada_part_done(s.name)
                    late.setdefault(s.length + 1, []).append(
                        lambda i: take_mod(layer, part0 + i, before + i + 1))

            dve.wait_ge(consts_in, 16 * 10)
            R = lambda k: prep[:, k, :]
            lr, li, ls, step, m1, m2, m3, cos, sin, cre, cim, m4, pr, pi = (R(k) for k in range(14))
            exp_small(step, ls, m1, m2, m3)
            link(V.tensor_tensor(ls, lr, step, ALU.mult))
            exp_small(mag[:], ls, m1, m2, m3)
            link(V.tensor_tensor(m1, li, step, ALU.mult))
            magic = 12582912.0
            link(V.tensor_scalar(m2, m1, 1.0 / (2 * math.pi), magic, ALU.mult, ALU.add))
            link(V.tensor_scalar(m2, m2, magic, None, ALU.subtract))
            c1 = 6.28125
            c2 = float(np.float32(np.floor((2 * math.pi - c1) * 2 ** 20) / 2 ** 20))
            c3 = float(2 * math.pi - c1 - c2)
            for c in (c1, c2, c3):
                link(V.scalar_tensor_tensor(out=m1, in0=m2, scalar=-c, in1=m1, op0=ALU.mult, op1=ALU.add))
            link(V.tensor_scalar(m1, m1, 0.5, None, ALU.mult))
            link(V.tensor_tensor(m2, m1, m1, ALU.mult))
            link(V.tensor_scalar(m3, m2, -1.0 / math.factorial(15), None, ALU.mult))
            for n in (13, 11, 9, 7, 5, 3):
                link(V.scalar_tensor_tensor(out=m3, in0=m3, scalar=(-1.0) ** (n // 2) / math.factorial(n), in1=m2,
                                            op0=ALU.add, op1=ALU.mult))
            link(V.scalar_tensor_tensor(out=m3, in0=m3, scalar=1.0, in1=m1, op0=ALU.add, op1=ALU.mult))
            link(V.tensor_scalar(m4, m2, 1.0 / math.factorial(16), None, ALU.mult))
            for n in (14, 12, 10, 8, 6, 4, 2):
                link(V.scalar_tensor_tensor(out=m4, in0=m4, scalar=(-1.0) ** (n // 2) / math.factorial(n), in1=m2,
                                            op0=ALU.add, op1=ALU.mult))
            link(V.tensor_scalar(m4, m4, 1.0, None, ALU.add))
            link(V.tensor_tensor(cos, m3, m3, ALU.mult))
            link(V.tensor_scalar(cos, cos, -2.0, 1.0, ALU.mult, ALU.add))
            link(V.scalar_tensor_tensor(out=sin, in0=m3, scalar=2.0, in1=m4, op0=ALU.mult, op1=ALU.mult))
            link(V.tensor_tensor(m1, mag[:], cos, ALU.mult))
            link(V.tensor_scalar(m1, m1, 1.0, None, ALU.subtract))
            link(V.tensor_tensor(m2, mag[:], sin, ALU.mult))
            link(V.tensor_tensor(m3, lr, lr, ALU.mult))
            link(V.tensor_tensor(m4, li, li, ALU.mult))
            link(V.tensor_tensor(m3, m3, m4, ALU.add))
            link(V.reciprocal(m3, m3))
            link(V.tensor_tensor(cre, m1, lr, ALU.mult))
            link(V.tensor_tensor(m4, m2, li, ALU.mult))
            link(V.tensor_tensor(cre, cre, m4, ALU.add))
            link(V.tensor_tensor(cre, cre, m3, ALU.mult))
            link(V.tensor_tensor(cim, m2, lr, ALU.mult))
            link(V.tensor_tensor(m4, m1, li, ALU.mult))
            link(V.tensor_tensor(cim, cim, m4, ALU.subtract))
            link(V.tensor_tensor(cim, cim, m3, ALU.mult))
            wide = lambda v, w: v.unsqueeze(2).broadcast_to([P, TILES, w])
            link(V.tensor_copy(pr, cos))
            link(V.tensor_copy(pi, sin))
            for re, im in ((0, 1), (4, 5)):
                link(V.memset(ef[:, :, re, 0:1], 1.0))
                link(V.memset(ef[:, :, im, 0:1], 0.0))
                for lg in range(4):
                    w = 1 << lg
                    ar, ai = ef[:, :, re, 0:w], ef[:, :, im, 0:w]
                    ta, tb = t8a[:, :, 0:w], t8b[:, :, 0:w]
                    link(V.tensor_tensor(ta, ar, wide(pr, w), ALU.mult))
                    link(V.tensor_tensor(tb, ai, wide(pi, w), ALU.mult))
                    link(V.tensor_tensor(ef[:, :, re, w:2 * w], ta, tb, ALU.subtract))
                    link(V.tensor_tensor(ta, ar, wide(pi, w), ALU.mult))
                    link(V.tensor_tensor(tb, ai, wide(pr, w), ALU.mult))
                    link(V.tensor_tensor(ef[:, :, im, w:2 * w], ta, tb, ALU.add))
                    link(V.tensor_tensor(m1, pr, pr, ALU.mult))
                    link(V.tensor_tensor(m2, pi, pi, ALU.mult))
                    link(V.scalar_tensor_tensor(out=pi, in0=pr, scalar=2.0, in1=pi, op0=ALU.mult, op1=ALU.mult))
                    link(V.tensor_tensor(pr, m1, m2, ALU.subtract))
            link(V.tensor_scalar(ef[:, :, 2, :], ef[:, :, 1, :], -1.0, None, ALU.mult))
            link(V.tensor_copy(ef[:, :, 3, :], ef[:, :, 0, :]))
            cr, ci = c_raw[:, :, 0, :], c_raw[:, :, 1, :]
            nr, ni = c_new[:, :, 0, :], c_new[:, :, 1, :]
            link(V.tensor_tensor(nr, cr, wide(cre, SC), ALU.mult))
            link(V.tensor_tensor(t16, ci, wide(cim, SC), ALU.mult))
            link(V.tensor_tensor(nr, nr, t16, ALU.subtract))
            link(V.tensor_tensor(ni, cr, wide(cim, SC), ALU.mult))
            link(V.tensor_tensor(t16, ci, wide(cre, SC), ALU.mult))
            V.scalar_tensor_tensor(out=ni, in0=ni, scalar=-1.0, in1=t16, op0=ALU.mult,
                                   op1=ALU.subtract).then_inc(prep_done, 1)
            while adds[0] < 2 * KT:
                ada_add(adds[0])
            take_mod(0, 1, 3)
            take_mod(0, 3, 4)

            def norm(number, mod_layer, shift, after):
                wait(dve, mod_ready, after)
                dve.wait_ge(mean_ready, number + 1)
                base = 10 * number
                if shift is None:
                    V.tensor_copy(hscale[:], gains[:, number, :]).then_inc(norm_link, 1)
                else:
                    V.scalar_tensor_tensor(out=hscale[:], in0=mod[:, mod_layer, shift + KT:shift + 2 * KT], scalar=1.0,
                                           in1=gains[:, number, :], op0=ALU.add, op1=ALU.mult).then_inc(norm_link, 1)
                V.tensor_scalar(meansq, norm_ps, EPS, None, ALU.add).then_inc(norm_link, 1)
                dve.wait_ge(root_ready, number + 1)
                V.reciprocal(rstd[:], rstd[:]).then_inc(norm_link, 1)
                dve.wait_ge(norm_link, base + 3)
                V.tensor_tensor(newton, rstd[:], rstd[:], ALU.mult).then_inc(norm_link, 1)
                dve.wait_ge(norm_link, base + 4)
                V.scalar_tensor_tensor(out=newton, in0=newton, scalar=-0.5, in1=meansq, op0=ALU.mult,
                                       op1=ALU.mult).then_inc(norm_link, 1)
                dve.wait_ge(norm_link, base + 5)
                V.scalar_tensor_tensor(out=rstd[:], in0=newton, scalar=1.5, in1=rstd[:], op0=ALU.add,
                                       op1=ALU.mult).then_inc(norm_link, 1)
                dve.wait_ge(norm_link, base + 6)
                for q in range(4):
                    if q >= 2:
                        if shift is None:
                            dve.wait_ge(out_done[q % 2], 16)
                        else:
                            dve.wait_ge(norm_lo, 4 * number + q - 1)
                    V.tensor_tensor(hf[:, q % 2], x[:, 4 * q:4 * q + 4, :],
                                    rstd[:].unsqueeze(1).broadcast_to([P, 4, T]), ALU.mult).then_inc(norm_link, 1)
                    dve.wait_ge(norm_link, base + 7 + q)
                    for k in range(4 * q, 4 * q + 4):
                        v = hf[:, q % 2, k % 4, :]
                        if shift is None:
                            V.tensor_scalar(v, v, hscale[:, k:k + 1], None, ALU.mult).then_inc(out_ready, 1)
                        else:
                            V.tensor_scalar(v, v, hscale[:, k:k + 1], mod[:, mod_layer, shift + k:shift + k + 1],
                                            ALU.mult, ALU.add).then_inc(norm_full, 1)

            dve.wait_ge(x_in, 16)
            norm(0, 0, 0, 4)
            s = st["qkv"]
            late = {}

            def softmax(hl):
                def f(i):
                    head = 2 * i + hl
                    slope = slopes[:, bass.ds(head, 1)]
                    dve.wait_ge(rel_in, 16)
                    dve.wait_ge(scores_done, head + 1)
                    wait(dve, p_turned, head)
                    V.scalar_tensor_tensor(out=s0, in0=rel[:, :, P:T], scalar=slope,
                                           in1=ps0[:, 0:NG * P].rearrange("p (g k) -> p g k", g=NG),
                                           op0=ALU.mult, op1=ALU.add).then_inc(s_biased, 1)
                    V.scalar_tensor_tensor(out=s1, in0=rel, scalar=slope,
                                           in1=ps1[:, 0:NG * T].rearrange("p (g k) -> p g k", g=NG),
                                           op0=ALU.mult, op1=ALU.add).then_inc(s_biased, 1)
                    dve.wait_ge(s_biased, 2 * head + 2)
                    V.tensor_reduce(small[:, 0:1], s0, AX.XY, ALU.max).then_inc(max_found, 1)
                    V.tensor_reduce(small[:, 1:2], s1, AX.XY, ALU.max).then_inc(max_found, 1)
                    dve.wait_ge(max_found, 2 * head + 2)
                    V.tensor_scalar(small[:, 2:4], small[:, 0:2], -SCALE, None, ALU.mult).then_inc(max_ready, 1)
                return f

            def denominators(hl):
                def f(i):
                    head = 2 * i + hl
                    dve.wait_ge(exp_done, 2 * head + 2)
                    wait(dve, mix_ready, 2 * head)
                    V.reciprocal(small[:, 6:8], small[:, 4:6]).then_inc(rden_ready, 1)
                return f

            def out_low(hl):
                def f(i):
                    head = 2 * i + hl
                    dve.wait_ge(o_hi, head + 1)
                    V.tensor_tensor(a_lo[:, head, :], pout[:, 0:T], a_hi[:, head, :].bitcast(F32),
                                    ALU.subtract).then_inc(o_lo, 1)
                return f
            for hl in range(2):
                late.setdefault(14 * hl + 14 + 7, []).append(softmax(hl))
                late.setdefault(14 * hl + 14 + 11, []).append(denominators(hl))
                late.setdefault(14 * hl + 14 + 18, []).append(out_low(hl))
            take_parts(s, late)
            run_steps(dve, s.count, s.length, low(s), late)

            def residual(name, layer, gate):
                s = st[name]
                late = {}
                dve.wait_ge(mod_ready, 12 if layer == 0 else 24)

                def add(b):
                    def f(i):
                        k = i * s.blocks + b
                        dve.wait_ge(piece_done, s.number(i, s.end_of[b]) + 1)
                        g = mod[:, layer, bass.ds(gate + k, 1)]
                        V.scalar_tensor_tensor(out=x[:, k, :], in0=proj[b % 2][:, 0:T], scalar=g, in1=x[:, k, :],
                                               op0=ALU.mult, op1=ALU.add).then_inc(block_out, 1)
                    return f

                for b in range(s.blocks):
                    late.setdefault(s.end_of[b] + 4, []).append(add(b))
                take_parts(s, late)
                run_steps(dve, s.count, s.length, low(s), late)

            def up(name, layer):
                s = st[name]
                pair0 = UPS[name]
                f0 = pair0 - 44 * layer
                late = {}

                def taps10(pl, side):
                    def f(i):
                        pair = pair0 + i * (s.blocks // 2) + pl
                        fb = f0 + i * (s.blocks // 2) + pl
                        cv = conv[:, pl % 2, side, :]

                        def tap(k):
                            return taps[:, fb, side, k:k + 1]
                        dve.wait_ge(conv0, 2 * pair + side + 1)
                        V.scalar_tensor_tensor(out=cv[:, 1:T], in0=proj[side][:, 0:T - 1], scalar=tap(1), in1=cv[:, 1:T],
                                               op0=ALU.mult, op1=ALU.add).then_inc(conv1, 1)
                        dve.wait_ge(conv1, 2 * pair + side + 1)
                        V.scalar_tensor_tensor(out=cv[:, 2:T], in0=proj[side][:, 0:T - 2], scalar=tap(0), in1=cv[:, 2:T],
                                               op0=ALU.mult, op1=ALU.add).then_inc(block_out, 1)
                        if side == 1:
                            dve.wait_ge(block_out, s.block(i, 2 * pl + 1) + 1)
                            dve.wait_ge(silu_ready, pair + 1)
                            wait(dve, act_lo, pair - 1)
                            V.tensor_tensor(gated[:, pl % 2, :], silu[:, pl % 2, :], cv, ALU.mult).then_inc(gated_ready, 1)
                    return f
                for pl in range(s.blocks // 2):
                    for side in range(2):
                        late.setdefault(4 * pl + 5 + 2 * side, []).append(taps10(pl, side))
                take_parts(s, late)
                run_steps(dve, s.count, s.length, low(s), late,
                          done=LO_FIRST * (name in ("up0a", "up1a")))

            def ffn(layer):
                dve.wait_ge(taps_in, 32 * (layer + 1))
                for h in "ab":
                    up(f"up{layer}{h}", layer)
                    up(f"up{layer}{h}_end", layer)
                    residual(f"down{layer}{h}", layer, 5 * KT)

            residual("attn_out", 0, 2 * KT)
            split_first("up0a")
            norm(1, 0, 3 * KT, 12)
            ffn(0)
            split_first("ssm_in")
            norm(2, 1, 0, 24)
            s = st["ssm_in"]
            late = {}

            def widen_b(b):
                def f(i):
                    n = 4 * i + b
                    dve.wait_ge(bc_in[b % 2], 16 * (2 * i + b // 2 + 1))
                    wait(dve, bu_done, 4 * (n - 1))
                    for g in range(2):
                        ins = V.tensor_scalar(b_wide[:, b % 2, :, g * SP_:(g + 1) * SP_], b_cur[:, b % 2],
                                              halves[:, 2 + g:3 + g], None, ALU.mult)
                    ins.then_inc(b_made, 1)
                return f

            def widen_c(b):
                def f(i):
                    n = 4 * i + b
                    dve.wait_ge(cc_in[b % 2], 16 * (2 * i + b // 2 + 1))
                    wait(dve, y_tile, 4 * (n - 1))
                    for g in range(2):
                        V.tensor_scalar(c_wide[:, b % 2, :, 0:2, g * SC:(g + 1) * SC], c_cur[:, b % 2],
                                        halves[:, g:g + 1], None, ALU.mult)
                        ins = V.tensor_scalar(c_wide[:, b % 2, :, 2, g * SC:(g + 1) * SC], c_cur[:, b % 2, :, 0, :],
                                              halves[:, g:g + 1], -1.0, ALU.mult, ALU.mult)
                    ins.then_inc(c_made, 1)
                return f

            def scan(tl):
                def f(i):
                    t = 16 * i + tl
                    p, q = tl % 2, tl % TABS
                    if tl == 0:
                        wait(dve, gelu_done, 4 * i - 1)
                    dve.wait_ge(rot_done, 2 * t + 2)
                    V.tensor_tensor(zin[:, p], zin[:, p], zin2[:, p], ALU.add).then_inc(zin_added, 1)
                    dve.wait_ge(zin_added, t + 1)
                    for ri in range(2):
                        V.tensor_tensor_scan(z[:, p, ri, :], mag[:, bass.ds(t, 1)].broadcast_to([P, T]), zin[:, p, ri, :],
                                             0.0, ALU.mult, ALU.add).then_inc(scanned, 1)
                    dve.wait_ge(scanned, 2 * t + 2)
                    wait(dve, y_tile, t - 1)
                    for k in range(2):
                        V.tensor_tensor(xs[:, p, 2 * k:2 * k + 2], z[:, p],
                                        tabs[q][:, k, :].unsqueeze(1).broadcast_to([P, 2, T]), ALU.mult).then_inc(xs_done, 1)
                return f

            def skip(b):
                def f(i):
                    n = 4 * i + b
                    dve.wait_ge(y_tile, 4 * n + 4)
                    if b:
                        wait(dve, gelu_done, n)
                    V.scalar_tensor_tensor(out=ypre[:, b % 2, :], in0=u[:, b, :], scalar=dskip[:, bass.ds(n, 1)],
                                           in1=y_ps[b % 2][:, 0:T], op0=ALU.mult, op1=ALU.add).then_inc(ypre_done, 1)
                return f
            for b in range(4):
                late.setdefault(2 * b + 3, []).append(widen_b(b))
                late.setdefault(2 * b + 5, []).append(widen_c(b))
                for q in range(4):
                    late.setdefault(2 * b + 6 + q // 2, []).append(scan(4 * b + q))
                late.setdefault(2 * b + 9, []).append(skip(b))
            run_steps(dve, s.count, s.length, low(s), late, done=LO_FIRST)
            s = st["gate"]
            late = {}

            def gate(b):
                def f(i):
                    n = 4 * i + b
                    dve.wait_ge(block_out, s.block(i, b) + 1)
                    dve.wait_ge(gf_ready, n + 1)
                    wait(dve, gg_lo, n - 1)
                    V.tensor_tensor(gmul[:, b % 2, :], gfull[:, b % 2, :], sig[:, b % 2, :], ALU.mult).then_inc(gm_ready, 1)
                return f
            for b in range(4):
                late.setdefault(2 * b + 5, []).append(gate(b))
            run_steps(dve, s.count, s.length, low(s), late)
            residual("ssm_out", 1, 2 * KT)
            split_first("up1a")
            norm(3, 1, 3 * KT, 24)
            ffn(1)
            norm(4, 1, None, 24)

        @block.gpsimd
        def _(pool):
            G = nc.gpsimd
            def square_step(k, number):
                n = KT * number + k
                if isinstance(k, int) and k == 0:
                    wait(pool, mean_ready, number)
                    G.tensor_tensor(sumsq[:], x[:, 0, :], x[:, 0, :], ALU.mult).then_inc(sumsq_made, 1)
                else:
                    pool.wait_ge(sumsq_made, n)
                    G.tensor_tensor(square[:], x[:, k, :], x[:, k, :], ALU.mult).then_inc(sq_made, 1)
                    pool.wait_ge(sq_made, n - number)
                    G.tensor_tensor(sumsq[:], sumsq[:], square[:], ALU.add).then_inc(sumsq_made, 1)

            def norm(number):
                for q in range(4):
                    pool.wait_ge(norm_hi, 4 * number + q + 1)
                    G.tensor_tensor(h_lo[:, 4 * q:4 * q + 4, :], hf[:, q % 2], h_hi[:, 4 * q:4 * q + 4, :].bitcast(F32),
                                    ALU.subtract).then_inc(norm_lo, 1)

            G.memset(ones[:], 1.0).then_inc(ones_ready, 1)
            for m in range(2 * KT):
                n = 2 * m
                pool.wait_ge(ada_scaled, m + 1)
                if m == 0:
                    G.tensor_copy(acc2, ada[:, n % ADA, :]).then_inc(ada_added, 1)
                elif m == KT:
                    pool.wait_ge(mod_summed, 1)
                    G.tensor_copy(acc2, ada[:, n % ADA, :]).then_inc(ada_added, 1)
                else:
                    pool.wait_ge(ada_added, m)
                    G.tensor_tensor(acc2, acc2, ada[:, n % ADA, :], ALU.add).then_inc(ada_added, 1)
                if m == 7:
                    pool.wait_ge(x_in, 16)
                if m >= 8 and m < 24:
                    square_step(m - 8, 0)
            norm(0)
            s = st["qkv"]
            late = {}

            def mix(hl):
                def f(i):
                    head = 2 * i + hl
                    pool.wait_ge(rden_ready, head + 1)
                    for n, v in ((0, s0), (1, s1)):
                        G.tensor_tensor(v[:, 0, :], v[:, 0, :], v[:, 1, :], ALU.add).then_inc(mix_link, 1)
                        pool.wait_ge(mix_link, 4 * head + 2 * n + 1)
                        G.tensor_tensor(v[:, 0, :], v[:, 0, :], v[:, 2, :], ALU.add).then_inc(mix_link, 1)
                        pool.wait_ge(mix_link, 4 * head + 2 * n + 2)
                        G.tensor_tensor(v[:, 0, :], v[:, 0, :], small[:, 6 + n:7 + n].broadcast_to([P, P + n * P]),
                                        ALU.mult).then_inc(mix_ready, 1)
                return f
            for hl in range(2):
                late.setdefault(14 * hl + 14 + 11, []).append(mix(hl))
            run_steps(pool, s.count, s.length, lambda i, j: None, late)

            def residual(name, norm_number):
                s = st[name]
                late = {}

                def sq(b):
                    def f(i):
                        k = i * s.blocks + b
                        pool.wait_ge(block_out, s.block(i, b) + 1)
                        square_step(k, norm_number)
                    return f

                def table(q):
                    def f(i):
                        per = s.length // TAB_EVERY
                        t = TAB0[name] + i * per + q
                        e = ef_in[:, q % 4]
                        if q % 4 == 0:
                            pool.wait_ge(ef_in_s[0], 4 * (t + 4))
                        fr = e[:, 4, :].unsqueeze(1).unsqueeze(3).broadcast_to([P, 2, 16, 16])
                        fi = e[:, 5, :].unsqueeze(1).unsqueeze(3).broadcast_to([P, 2, 16, 16])
                        ea = e[:, 0:2, :].unsqueeze(2).broadcast_to([P, 2, 16, 16])
                        eb = e[:, 2:4, :].unsqueeze(2).broadcast_to([P, 2, 16, 16])
                        wait(pool, tab_made, t)
                        G.tensor_tensor(tab_a, fr, ea, ALU.mult).then_inc(tab_link, 1)
                        G.tensor_tensor(tab_b, fi, eb, ALU.mult).then_inc(tab_link, 1)
                        pool.wait_ge(tab_link, 2 * t + 2)
                        wait(pool, tab_out[q % 2], (TAB0[name] // 2 + i * (per // 2) + q // 2) * 16)
                        G.tensor_tensor(tab_o[:, q % 2, :].rearrange("p (c a b) -> p c a b", c=2, a=16), tab_a, tab_b,
                                        ALU.add).then_inc(tab_made, 1)
                    return f
                if name in TAB0:
                    for q in range(s.length // TAB_EVERY):
                        late.setdefault(TAB_EVERY * q + 5, []).append(table(q))
                if norm_number:
                    for b in range(s.blocks):
                        late.setdefault(s.end_of[b] + 4, []).append(sq(b))
                run_steps(pool, s.count, s.length, lambda i, j: None, late)

            def up(name):
                s = st[name]
                pair0 = UPS[name]
                late = {}

                def low_act(pl):
                    def f(i):
                        pair = pair0 + i * (s.blocks // 2) + pl
                        dst = pair0 % HALF + i * (s.blocks // 2) + pl
                        pool.wait_ge(act_hi, pair + 1)
                        G.tensor_tensor(a_lo[:, dst, :], gated[:, pl % 2, :], a_hi[:, dst, :].bitcast(F32),
                                        ALU.subtract).then_inc(act_lo, 1)
                    return f
                for pl in range(s.blocks // 2):
                    late.setdefault(4 * pl + 9, []).append(low_act(pl))
                run_steps(pool, s.count, s.length, lambda i, j: None, late)

            def ffn(layer, norm_number):
                for h in "ab":
                    up(f"up{layer}{h}")
                    up(f"up{layer}{h}_end")
                    residual(f"down{layer}{h}", norm_number if h == "b" else 0)

            residual("attn_out", 1)
            norm(1)
            ffn(0, 2)
            norm(2)
            s = st["ssm_in"]
            late = {}

            def rotate(tl):
                def f(i):
                    t = 16 * i + tl
                    p, q = tl % 2, tl % TABS
                    pool.wait_ge(tabs_in[q], 16 * (16 // TABS * i + tl // TABS + 1))
                    pool.wait_ge(bu_copied, 2 * t + 2)
                    wait(pool, scanned, 2 * (t - 1))
                    G.tensor_tensor(zin[:, p], bu[:, p, 0:2, :], tabs[q][:, 0, :].unsqueeze(1).broadcast_to([P, 2, T]),
                                    ALU.mult).then_inc(rot_done, 1)
                    G.tensor_tensor(zin2[:, p], bu[:, p, 1:3, :], tabs[q][:, 1, :].unsqueeze(1).broadcast_to([P, 2, T]),
                                    ALU.mult).then_inc(rot_done, 1)
                return f

            def g_low(b):
                def f(i):
                    n = 4 * i + b
                    pool.wait_ge(g_hi, n + 1)
                    G.tensor_tensor(a_lo[:, n, :], geluo[:, b % 2, :], a_hi[:, n, :].bitcast(F32),
                                    ALU.subtract).then_inc(g_lo, 1)
                return f
            for b in range(4):
                for q in range(4):
                    late.setdefault(2 * b + 6 + q // 2, []).append(rotate(4 * b + q))
                late.setdefault(min(2 * b + 10, 15), []).append(g_low(b))
            run_steps(pool, s.count, s.length, lambda i, j: None, late)
            s = st["gate"]
            late = {}

            def whole(b):
                def f(i):
                    n = 4 * i + b
                    wait(pool, gm_ready, n - 1)
                    G.tensor_tensor(gfull[:, b % 2, :], a_hi[:, n, :].bitcast(F32), a_lo[:, n, :].bitcast(F32),
                                    ALU.add).then_inc(gf_ready, 1)
                return f

            def gate_low(b):
                def f(i):
                    n = 4 * i + b
                    pool.wait_ge(gg_hi, n + 1)
                    G.tensor_tensor(h_lo[:, n, :], gmul[:, b % 2, :], h_hi[:, n, :].bitcast(F32),
                                    ALU.subtract).then_inc(gg_lo, 1)
                return f
            for b in range(4):
                late.setdefault(2 * b + 4, []).append(whole(b))
                late.setdefault(2 * b + 7, []).append(gate_low(b))
            run_steps(pool, s.count, s.length, lambda i, j: None, late)
            residual("ssm_out", 3)
            norm(3)
            ffn(1, 4)

        @block.tensor
        def _(pe):
            mm = nc.tensor.matmul

            def products(s, hi, lo, ready):
                def f(i, j):
                    b, k0, nk, last = s.pieces[j]
                    n = s.number(i, j)
                    if k0 == 0:
                        wait(pe, block_out, s.block(i, b) - 1)
                    pe.wait_ge(lo_ready, n + 1)
                    if isinstance(i, int):
                        ready(k0 + nk)
                    o = proj[b % 2][:, 0:T]
                    for k in range(k0, k0 + nk):
                        w = slice((k - k0) * P, (k - k0 + 1) * P)
                        mm(o, w_hi[:, j % LAG, w], hi[:, k, :], start=(k == 0), stop=False)
                        mm(o, w_hi[:, j % LAG, w], lo[:, k, :], start=False, stop=False)
                        ins = mm(o, w_lo[:, j % LAG, w], hi[:, k, :], start=False, stop=last and k == k0 + nk - 1)
                    ins.then_inc(piece_done, 1)
                return f

            def sum_part(v, done, *sources):
                for sem_, value in sources:
                    pe.wait_ge(sem_, value)
                wait(pe, mod_ready, done)
                for c in range(MODB):
                    ins = mm(mod_ps[:, c:c + 1], v[:, c * P:(c + 1) * P], ones[:, 0:1], start=True, stop=True)
                ins.then_inc(mod_summed, 1)

            def sum_parts(s, late):
                if s.ada:
                    before = ada_part_done(s.name)


                    def f(i):
                        if s.name == "qkv":
                            pe.wait_ge(v_ready, 2 * i + 1)
                        sum_part(acc, before + i, (ada_used, 2 * KT + KT * (before + i - 4) + KT))
                    late.setdefault(s.length - 3, []).append(f)

            def norm(number):
                pe.wait_ge(sumsq_made, KT * (number + 1))
                mm(norm_ps, mean_w[:], sumsq[:], start=True, stop=True).then_inc(mean_ready, 1)

            def h_ready(number):
                return lambda k: pe.wait_ge(norm_lo, 4 * number + -(-k // 4))

            pe.wait_ge(consts_in, 16 * 10)
            pe.wait_ge(ones_ready, 1)
            sum_part(acc2, 0, (ada_added, KT))
            sum_part(acc, 1, (ada_used, KT))
            sum_part(acc2, 2, (ada_added, 2 * KT))
            sum_part(acc, 3, (ada_used, 2 * KT))
            norm(0)
            s = st["qkv"]
            late = {}

            def scores(hl):
                def f(i):
                    head = 2 * i + hl
                    pe.wait_ge(block_out, 7 * head + 7)
                    wait(pe, s_biased, 2 * head)
                    for g in range(NG):
                        mm(ps0[:, g * P:(g + 1) * P], qk[:, hl, g, 0:P], qk[:, hl, NG + g, 0:P], start=True, stop=True)
                    for g in range(NG):
                        ins = mm(ps1[:, g * T:(g + 1) * T], qk[:, hl, g, P:T], qk[:, hl, NG + g, :], start=True, stop=True)
                    ins.then_inc(scores_done, 1)
                    wait(pe, v_ready, head)
                    pe.wait_ge(mod_ready, 4 + i + hl)
                    for b in range(2):
                        ins = nc.tensor.transpose(pmisc[:, b * P:(b + 1) * P], v_t[:, b * P:(b + 1) * P], ident[:])
                    ins.then_inc(v_turned, 1)
                return f

            def turn(hl):
                def f(i):
                    head = 2 * i + hl
                    pe.wait_ge(mix_ready, 2 * head + 2)
                    wait(pe, p_copied, head)
                    for c, v in enumerate((s0[:, 0, :], s1[:, 0, 0:P], s1[:, 0, P:T])):
                        ins = nc.tensor.transpose(pturn[:, c * P:(c + 1) * P], v, ident[:])
                    ins.then_inc(p_turned, 1)
                return f

            def values(hl):
                def f(i):
                    head = 2 * i + hl
                    pe.wait_ge(p_copied, head + 1)
                    pe.wait_ge(v_ready, head + 1)
                    wait(pe, o_lo, head)
                    mm(pout[:, 0:T], v_sb[:, 0, :], p_t[:, 0:T], start=True, stop=False)
                    mm(pout[:, P:T], v_sb[:, 1, :], p_t[:, T:T + P], start=False, stop=True).then_inc(pv_done, 1)
                return f
            for hl in range(2):
                late.setdefault(14 * hl + 14 + 3, []).append(scores(hl))
                late.setdefault(14 * hl + 14 + 11, []).append(turn(hl))
                late.setdefault(14 * hl + 14 + 13, []).append(values(hl))
            sum_parts(s, late)
            run_steps(pe, s.count, s.length, products(s, h_hi, h_lo, h_ready(0)), late)

            def stream(name, hi, lo, ready):
                s = st[name]
                late = {}
                sum_parts(s, late)
                run_steps(pe, s.count, s.length, products(s, hi, lo, ready), late)

            def ffn(layer, number):
                for half, h in enumerate("ab"):
                    stream(f"up{layer}{h}", h_hi, h_lo, h_ready(number))
                    stream(f"up{layer}{h}_end", h_hi, h_lo, h_ready(number))
                    before = FB * layer + HALF * half
                    stream(f"down{layer}{h}", a_hi, a_lo, lambda k: pe.wait_ge(act_lo, before + k))

            stream("attn_out", a_hi, a_lo, lambda k: pe.wait_ge(o_lo, k))
            norm(1)
            ffn(0, 1)
            norm(2)
            s = st["ssm_in"]
            late = {}

            def b_u(tl):
                def f(i):
                    t = 16 * i + tl
                    b, q = divmod(tl, 4)
                    if q == 0:
                        pe.wait_ge(b_made, 4 * i + b + 1)
                        pe.wait_ge(block_out, s.block(i, b) + 1)
                    wait(pe, bu_copied, 2 * (t - 3))
                    rows = slice(32 * q, 32 * q + 32)
                    for ri in range(2):
                        ins = mm(bu_ps[tl % 4][:, ri * T:(ri + 1) * T], b_wide[rows, b % 2, ri, :], u[rows, b, :],
                                 start=True, stop=True)
                    ins.then_inc(bu_done, 1)
                return f

            def c_x(tl):
                def f(i):
                    t = 16 * i + tl
                    b, q = divmod(tl, 4)
                    n = 4 * i + b
                    if q == 0:
                        pe.wait_ge(c_made, n + 1)
                        if b != 1:
                            wait(pe, ypre_done, n - 1)
                    if tl == 2:
                        wait(pe, ypre_done, 4 * i)
                    pe.wait_ge(xs_done, 2 * t + 2)
                    o = y_ps[b % 2][32 * q:32 * q + 32, 0:T]
                    for k, part in enumerate((0, 1, 1, 2)):
                        ins = mm(o, c_wide[:, b % 2, q, part, :], xs[:, tl % 2, k, :], start=(k == 0), stop=(k == 3))
                    ins.then_inc(y_tile, 1)
                return f
            for b in range(4):
                for q in range(4):
                    late.setdefault(2 * b + 4 + q // 2, []).append(b_u(4 * b + q))
                for q in range(4):
                    late.setdefault(2 * b + 6 + q // 2, []).append(c_x(4 * b + q))
            run_steps(pe, s.count, s.length, products(s, h_hi, h_lo, h_ready(2)), late)
            stream("gate", a_hi, a_lo, lambda k: pe.wait_ge(g_lo, k))
            stream("ssm_out", h_hi, h_lo, lambda k: pe.wait_ge(gg_lo, k))
            norm(3)
            ffn(1, 3)
            norm(4)


_OUT = (P, KT, T)


def kernel(**inputs):
    import concourse.bacc as _bacc
    from concourse.bass_utils import run_bass_kernel_spmd as _run

    v = {k: np.asarray(x) for k, x in inputs.items()}
    cols = lambda m: m.reshape(*m.shape[:-1], -1, P)
    blocks = lambda w: w.reshape(w.shape[0] // P, P, w.shape[1] // P, P).transpose(2, 1, 0, 3)
    flat = lambda w: np.ascontiguousarray(w).reshape(*w.shape[:-2], -1)
    L = v["ada_w"].shape[0]
    arrays = {
        "x": v["x"][0].T.reshape(KT, P, T).transpose(1, 0, 2),
        "c": cols(v["c"])[0].T,
        "ada_w": v["ada_w"],
        "ada_b": cols(v["ada_b"]).transpose(2, 0, 1),
        "gains": np.stack([v["norm1_g"][0], v["norm2_g"][0], v["norm1_g"][1], v["norm2_g"][1], v["final_norm_g"]])
        .reshape(5, KT, P).transpose(2, 0, 1),
        "w_in": flat(blocks(v["attn_w_in"][0]).reshape(7, HEADS, P, KT, P).transpose(1, 0, 2, 3, 4)),
        "w_out": flat(blocks(v["attn_w_out"][0])),
        "ssm_w_in": flat(blocks(v["ssm_w_in"][0])),
        "ssm_w_gate": flat(blocks(v["ssm_w_gate"][0])),
        "ssm_w_out": flat(blocks(v["ssm_w_out"][0])),
        "w_up": np.stack([flat(blocks(v["ffn_w_up"][l]).reshape(2, FB, P, KT, P).transpose(1, 0, 2, 3, 4))
                          for l in range(L)]),
        "w_down": np.stack([np.stack([flat(blocks(v["ffn_w_down"][l][h * HALF * P:(h + 1) * HALF * P]))
                                      for h in range(2)]) for l in range(L)]),
        "conv_w": v["ffn_conv_w"].reshape(L, 3, 2, FB, P).transpose(0, 4, 3, 2, 1),
        "conv_b": v["ffn_conv_b"].reshape(L, 2, FB, P).transpose(0, 3, 2, 1),
        "ssm_d": cols(v["ssm_d"])[0].T,
        "ssm_p": np.stack([m.reshape(TILES, P).T for m in (
            v["ssm_a_re"][0], v["ssm_a_im"][0], np.repeat(v["ssm_log_step"][0][:, None], SP_, 1))], 1),
        "ssm_b": np.stack([m.reshape(KT, 8, SP_, SC).transpose(0, 1, 3, 2).reshape(KT, P, SP_)
                           for m in (v["ssm_b_re"][0], v["ssm_b_im"][0])], 2),
        "ssm_c": np.stack([m.reshape(TILES, 2, SC, SP_).transpose(1, 3, 0, 2).reshape(P, TILES, SC)
                           for m in (v["ssm_c_re"][0], v["ssm_c_im"][0])], 2),
    }
    t = np.arange(P)[:, None, None] + P
    dist = t - np.arange(T)[None, None, :]
    dil = np.array([d for _, d in GROUPS])[None, :, None]
    span = np.array([w // d for w, d in GROUPS])[None, :, None]
    seen = (dist >= 0) & (dist % dil == 0) & (dist <= span * dil)
    arrays["rel"] = np.where(seen, -dist, NEG).astype(np.float32)
    slope = 2.0 ** (-8.0 * np.arange(1, HEADS + 1) / HEADS) / SCALE
    arrays["slopes"] = np.tile(slope.astype(np.float32), (P, 1))
    p = np.arange(P)
    arrays["halves"] = np.stack([p < SP_, p >= SP_, (p // SC) % 2 == 0, (p // SC) % 2 == 1], 1).astype(np.float32)
    arrays["ident"] = np.eye(P, dtype=np.float32)
    arrays["mean_w"] = np.full((P, P), 1.0 / D, np.float32)

    nc = _bacc.Bacc("TRN2", target_bir_lowering=False, num_devices=1)
    aps, maps = {}, {}
    for name, m in arrays.items():
        maps["in_" + name] = m = np.ascontiguousarray(m)
        aps[name] = nc.dram_tensor("in_" + name, m.shape, F32, kind="ExternalInput").ap()
    aps["ada_w"] = aps["ada_w"].rearrange("l (k p) (h n) -> l k h p n", p=P, n=MODW)
    out = nc.dram_tensor("out", _OUT, F32, kind="ExternalOutput").ap()
    build(nc, aps, out)
    r = _run(nc, [maps], core_ids=[0])
    return r.results[0]["out"].transpose(1, 0, 2).reshape(D, T).T[None]
```
